# Optimizing a Trainium2 kernel written in Bass

```python
import jax, jax.numpy as jnp
from jax import lax
import numpy as np

D_MODEL = 2048
BATCH = 1
SEQ = 256
DEPTH = 1
DEC_BATCH = 1
DEC_SEQ = 64
PAST_LEN = 128

CHUNK = 64
N_PAST_CHUNKS = 8
A_REACH = N_PAST_CHUNKS * CHUNK
HEAD_DIM = 128
H_A = 8
H_B = 8
W_A = H_A * HEAD_DIM
W_B = H_B * HEAD_DIM
REL_CLIP = 128
N_REL = 2 * REL_CLIP + 1
D_FF = 4 * D_MODEL
D_PLE = 256
Q_BLOCK = 128
RMS_EPS = 1e-6
D_IN = 3 * W_A + 3 * W_B + H_B + 2 * D_MODEL
SPLITS = [int(s) for s in np.cumsum([W_A, W_A, W_A, W_B, W_B, W_B, H_B, D_MODEL])]
SCALE = HEAD_DIM ** -0.5
NEG = -1e30

kernel_name = 'hybrid_chunkband_fox_stream_step'

def rmsnorm(x, g):
    x32 = x.astype(jnp.float32)
    y = x32 * lax.rsqrt(jnp.mean(x32 * x32, axis=-1, keepdims=True) + RMS_EPS)
    return (y * g.astype(jnp.float32)).astype(x.dtype)

def heads(t, h):
    return t.reshape(t.shape[:-1] + (h, HEAD_DIM))

def mix_inputs(h, g_mix, w_in, b_f):
    n = rmsnorm(h, g_mix)
    u = n @ w_in
    qa, ka, va, qb, kb, vb, fl, ga, gb = jnp.split(u, SPLITS, axis=-1)
    logf = jax.nn.log_sigmoid(fl.astype(jnp.float32) + b_f.astype(jnp.float32))
    return (heads(qa, H_A), heads(ka, H_A), heads(va, H_A),
            heads(qb, H_B), heads(kb, H_B), heads(vb, H_B), logf, ga, gb)

def rel_bias_lookup(table, dist):
    idx = np.clip(dist, -REL_CLIP, REL_CLIP) + REL_CLIP
    return jnp.take(table.astype(jnp.float32), jnp.asarray(idx), axis=1)

def band_attn_prompt(q, k, v, table):
    b, s, h, d = q.shape
    nc = s // CHUNK
    n_off = N_PAST_CHUNKS + 1
    qc = q.reshape(b, nc, CHUNK, h, d)
    pad = jnp.zeros((b, A_REACH, h, d), k.dtype)
    kp = jnp.concatenate([pad, k], axis=1).reshape(b, nc + N_PAST_CHUNKS, CHUNK, h, d)
    vp = jnp.concatenate([pad.astype(v.dtype), v], axis=1).reshape(b, nc + N_PAST_CHUNKS, CHUNK, h, d)
    scores = jnp.concatenate(
        [jnp.einsum('bcihd,bcjhd->bhcij', qc, kp[:, j:j + nc]) for j in range(n_off)],
        axis=-1).astype(jnp.float32) * SCALE
    kk = np.arange(n_off * CHUNK)
    k_chunk = kk // CHUNK - N_PAST_CHUNKS
    k_pos = k_chunk * CHUNK + kk % CHUNK
    q_pos = np.arange(CHUNK)
    bias = rel_bias_lookup(table, q_pos[:, None] - k_pos[None, :])
    valid = (np.arange(nc)[:, None] + k_chunk[None, :]) >= 0
    scores = jnp.where(valid[None, None, :, None, :], scores + bias[:, None], NEG)
    probs = jax.nn.softmax(scores, axis=-1).astype(v.dtype)
    out = sum(jnp.einsum('bhcij,bcjhd->bcihd', probs[..., j * CHUNK:(j + 1) * CHUNK], vp[:, j:j + nc])
              for j in range(n_off))
    return out.reshape(b, s, h, d)

def band_attn_sample(q, k_new, v_new, k_cache, v_cache, table):
    t = q.shape[1]
    L = k_cache.shape[1]
    k = jnp.concatenate([k_cache.astype(k_new.dtype), k_new], axis=1)
    v = jnp.concatenate([v_cache.astype(v_new.dtype), v_new], axis=1)
    scores = jnp.einsum('bqhd,bkhd->bhqk', q, k).astype(jnp.float32) * SCALE
    k_pos = np.concatenate([np.arange(L) - L, np.arange(t)])
    bias = rel_bias_lookup(table, np.arange(t)[:, None] - k_pos[None, :])
    probs = jax.nn.softmax(scores + bias[None], axis=-1).astype(v.dtype)
    out = jnp.einsum('bhqk,bkhd->bqhd', probs, v)
    return out, k[:, -L:], v[:, -L:]

def fox_prompt(q, k, v, logf):
    b, s, h, d = q.shape
    nb = s // Q_BLOCK
    Fk = jnp.cumsum(logf, axis=1).transpose(0, 2, 1)
    qb = q.reshape(b, nb, Q_BLOCK, h, d).transpose(1, 0, 2, 3, 4)
    Fq = Fk.reshape(b, h, nb, Q_BLOCK).transpose(2, 0, 1, 3)
    qpos = jnp.arange(s).reshape(nb, Q_BLOCK)
    kpos = jnp.arange(s)

    def block(args):
        qi, fqi, pi = args
        sc = (jnp.einsum('bqhd,bkhd->bhqk', qi, k).astype(jnp.float32) * SCALE
              + (fqi[..., None] - Fk[:, :, None, :]))
        sc = jnp.where(pi[:, None] >= kpos[None, :], sc, NEG)
        p = jax.nn.softmax(sc, axis=-1).astype(v.dtype)
        return jnp.einsum('bhqk,bkhd->bqhd', p, v)

    out = lax.map(block, (qb, Fq, qpos))
    return out.transpose(1, 0, 2, 3, 4).reshape(b, s, h, d)

def fox_sample(q, k_new, v_new, lf_new, k_cache, v_cache, lf_cache):
    t = q.shape[1]
    L = k_cache.shape[1]
    k = jnp.concatenate([k_cache.astype(k_new.dtype), k_new], axis=1)
    v = jnp.concatenate([v_cache.astype(v_new.dtype), v_new], axis=1)
    lf = jnp.concatenate([lf_cache.astype(jnp.float32), lf_new], axis=1)
    F = jnp.cumsum(lf, axis=1).transpose(0, 2, 1)
    sc = (jnp.einsum('bqhd,bkhd->bhqk', q, k).astype(jnp.float32) * SCALE
          + (F[:, :, L:, None] - F[:, :, None, :]))
    mask = (L + np.arange(t))[:, None] >= np.arange(L + t)[None, :]
    sc = jnp.where(mask[None, None], sc, NEG)
    p = jax.nn.softmax(sc, axis=-1).astype(v.dtype)
    return jnp.einsum('bhqk,bkhd->bqhd', p, v)

def finish_layer(h, oa, ob, ga, gb, ple, w_a_proj, w_b_proj, w_o, g_mlp, w_up, w_down,
                 g_ple, w_ple_gate, w_ple_proj):
    ya = oa.reshape(oa.shape[:2] + (W_A,)) @ w_a_proj
    yb = ob.reshape(ob.shape[:2] + (W_B,)) @ w_b_proj
    m = jax.nn.sigmoid(ga) * ya + jax.nn.sigmoid(gb) * yb
    h = h + m @ w_o
    a = rmsnorm(h, g_mlp) @ w_up
    h = h + jnp.square(jax.nn.relu(a)) @ w_down
    gate = jax.nn.sigmoid(rmsnorm(h, g_ple) @ w_ple_gate)
    return h + (ple.astype(h.dtype) @ w_ple_proj) * gate

def setup_inputs(seed: int = 0) -> dict:
    key = jax.random.key(seed)
    ks = jax.random.split(key, 32)
    f32 = jnp.float32
    la = min(A_REACH, PAST_LEN)

    def nrm(k, shape, scale=1.0):
        return jax.random.normal(k, shape, f32) * scale

    def gain(k, shape):
        return 1.0 + 0.05 * jax.random.normal(k, shape, f32)

    return {
        'x_prompt': nrm(ks[0], (BATCH, SEQ, D_MODEL)),
        'x_sample': nrm(ks[1], (DEC_BATCH, DEC_SEQ, D_MODEL)),
        'p_prompt': nrm(ks[2], (DEPTH, BATCH, SEQ, D_PLE)),
        'p_sample': nrm(ks[3], (DEPTH, DEC_BATCH, DEC_SEQ, D_PLE)),
        'cache_a_k': nrm(ks[4], (DEPTH, DEC_BATCH, la, H_A, HEAD_DIM)),
        'cache_a_v': nrm(ks[5], (DEPTH, DEC_BATCH, la, H_A, HEAD_DIM)),
        'cache_b_k': nrm(ks[6], (DEPTH, DEC_BATCH, PAST_LEN, H_B, HEAD_DIM)),
        'cache_b_v': nrm(ks[7], (DEPTH, DEC_BATCH, PAST_LEN, H_B, HEAD_DIM)),
        'cache_b_logf': jax.nn.log_sigmoid(3.0 + nrm(ks[8], (DEPTH, DEC_BATCH, PAST_LEN, H_B))),
        'g_mix': gain(ks[9], (DEPTH, D_MODEL)),
        'w_in': nrm(ks[10], (DEPTH, D_MODEL, D_IN), D_MODEL ** -0.5),
        'b_f': 3.0 + 0.5 * jax.random.normal(ks[11], (DEPTH, H_B), f32),
        'rel_bias': nrm(ks[12], (DEPTH, H_A, N_REL), 0.1),
        'w_a_proj': nrm(ks[13], (DEPTH, W_A, D_MODEL), W_A ** -0.5),
        'w_b_proj': nrm(ks[14], (DEPTH, W_B, D_MODEL), W_B ** -0.5),
        'w_o': nrm(ks[15], (DEPTH, D_MODEL, D_MODEL), D_MODEL ** -0.5),
        'g_mlp': gain(ks[16], (DEPTH, D_MODEL)),
        'w_up': nrm(ks[17], (DEPTH, D_MODEL, D_FF), D_MODEL ** -0.5),
        'w_down': nrm(ks[18], (DEPTH, D_FF, D_MODEL), D_FF ** -0.5),
        'g_ple': gain(ks[19], (DEPTH, D_MODEL)),
        'w_ple_gate': nrm(ks[20], (DEPTH, D_MODEL, D_MODEL), D_MODEL ** -0.5),
        'w_ple_proj': nrm(ks[21], (DEPTH, D_PLE, D_MODEL), D_PLE ** -0.5),
        'g_final': gain(ks[22], (D_MODEL,)),
    }

def reference(x_prompt, x_sample, p_prompt, p_sample, cache_a_k, cache_a_v, cache_b_k,
              cache_b_v, cache_b_logf, g_mix, w_in, b_f, rel_bias, w_a_proj, w_b_proj, w_o,
              g_mlp, w_up, w_down, g_ple, w_ple_gate, w_ple_proj, g_final):
    sa_kp, sa_vp, sb_kp, sb_vp, sb_lp = [], [], [], [], []
    sa_ks, sa_vs, sb_ks, sb_vs, sb_ls = [], [], [], [], []
    hp, hs = x_prompt, x_sample
    for i in range(DEPTH):
        qa, ka, va, qb, kb, vb, lf, ga, gb = mix_inputs(hp, g_mix[i], w_in[i], b_f[i])
        oa = band_attn_prompt(qa, ka, va, rel_bias[i])
        ob = fox_prompt(qb, kb, vb, lf)
        la = min(A_REACH, hp.shape[1])
        sa_kp.append(ka[:, -la:])
        sa_vp.append(va[:, -la:])
        sb_kp.append(kb)
        sb_vp.append(vb)
        sb_lp.append(lf)
        hp = finish_layer(hp, oa, ob, ga, gb, p_prompt[i], w_a_proj[i], w_b_proj[i], w_o[i],
                          g_mlp[i], w_up[i], w_down[i], g_ple[i], w_ple_gate[i], w_ple_proj[i])
        qa, ka, va, qb, kb, vb, lf, ga, gb = mix_inputs(hs, g_mix[i], w_in[i], b_f[i])
        oa, nka, nva = band_attn_sample(qa, ka, va, cache_a_k[i], cache_a_v[i], rel_bias[i])
        ob = fox_sample(qb, kb, vb, lf, cache_b_k[i], cache_b_v[i], cache_b_logf[i])
        sa_ks.append(nka)
        sa_vs.append(nva)
        sb_ks.append(kb)
        sb_vs.append(vb)
        sb_ls.append(lf)
        hs = finish_layer(hs, oa, ob, ga, gb, p_sample[i], w_a_proj[i], w_b_proj[i], w_o[i],
                          g_mlp[i], w_up[i], w_down[i], g_ple[i], w_ple_gate[i], w_ple_proj[i])
    y_prompt = rmsnorm(hp, g_final)
    y_sample = rmsnorm(hs, g_final)
    return (y_prompt, y_sample,
            jnp.stack(sa_kp), jnp.stack(sa_vp), jnp.stack(sb_kp), jnp.stack(sb_vp), jnp.stack(sb_lp),
            jnp.stack(sa_ks), jnp.stack(sa_vs), jnp.stack(sb_ks), jnp.stack(sb_vs), jnp.stack(sb_ls))


_drawn_inputs = setup_inputs


def setup_inputs(seed=0):
    import zlib

    import numpy as np

    out = dict(_drawn_inputs(seed))
    spreads = {}
    factors = {'cache_b_logf': 20.643, 'rel_bias': 7.67, 'g_ple': 22.38}
    for name, (base, spread) in spreads.items():
        noise = np.random.default_rng([zlib.crc32(name.encode()), seed]).standard_normal(out[name].shape)
        drawn = base * np.exp(spread * noise) if base else spread * noise
        out[name] = __import__('jax').numpy.asarray(drawn.astype(out[name].dtype))
    for name, factor in factors.items():
        out[name] = (out[name] * factor).astype(out[name].dtype)
    return out
```

```python
import numpy as np

import concourse.bass as bass
from concourse import mybir

F32 = mybir.dt.float32
F32R = mybir.dt.float32r
ALU = mybir.AluOpType
ACT = mybir.ActivationFunctionType
AX_X = mybir.AxisListType.X

P = 128
D_MODEL = 2048
HEADS = 8
HD = 128
PAST = 128
NEW = 64
SEQ = 256
TOK = NEW + SEQ
KEYS = PAST + TOK
KB = D_MODEL // P
D_FF = 4 * D_MODEL
QUARTERS = D_FF // D_MODEL
D_PLE = 256
CHUNK = 64
SLAB_KB = 8
SLAB = SLAB_KB * P
SLOTS = 4
EPS = 1e-6
SCALE = HD ** -0.5
NEG = -1e30
REL_CLIP = 128
BIAS_ROW = 384

S0, S1 = 0, PAST + NEW
P0, P1, P2 = S1, S1 + P, S1 + P + SEQ

UNITS = 2 * HEADS
T_FORGET = 0
T_UNIT = 1
T_MERGE = T_UNIT + 3 * UNITS
T_OUT = T_MERGE + 3 * KB
T_FF = T_OUT + KB
T_PLE = T_FF + QUARTERS * 2 * KB
T_GATE = T_PLE + 2
T_END = T_GATE + KB

MIX, MLP, PLE, FINAL = range(4)
Y_CHUNKS = ((0, 4, 0), (11, 3, 1), (4, 4, 0), (14, 2, 1), (8, 3, 0))


class Panel:

    def __init__(self, first, stride=0, turn=0):
        self.first, self.stride, self.turn = first, stride, turn
        self.half = first % 2

    def plus(self, n):
        return Panel(self.first + n, self.stride, self.turn)

    def count(self, per=1, add=0):
        fixed = per * self.first + add
        return fixed + self.turn * (per * self.stride) if self.stride else fixed

    def loads(self):
        fixed = 16 * (self.first // 2 + 1)
        return fixed + self.turn * (8 * self.stride) if self.stride else fixed


class Unit:

    def __init__(self, head, mixer):
        self.head, self.mixer = head, mixer

    def count(self, per=1, add=0):
        return self.head * (2 * per) + (per * self.mixer + add)


def hybrid_layer(nc, io):
    from contextlib import ExitStack

    with ExitStack() as ctx:
        def sb(name, shape, dt=F32):
            return ctx.enter_context(nc.sbuf_tensor(name, shape, dt))

        def sem(name):
            return ctx.enter_context(nc.semaphore(name))

        def under(name, shape):
            guard = nc.sbuf_tensor(name, shape, F32)
            t = guard.__enter__()
            guard.__exit__(None, None, None)
            return t

        w_raw = sb("w_raw", [P, SLOTS, SLAB])
        w_hi = sb("w_hi", [P, SLOTS, SLAB], F32R)
        w_lo = sb("w_lo", [P, SLOTS, SLAB], F32R)
        x_hi = sb("x_hi", [P, KB * TOK], F32R)
        x_lo = sb("x_lo", [P, KB * TOK], F32R)
        ple_part = under("ple_part", [P, KB * TOK])
        o_hi = sb("o_hi", [P, KB * TOK], F32R)
        o_lo = sb("o_lo", [P, KB * TOK], F32R)
        m_hi = sb("m_hi", [P, KB * TOK], F32R)
        m_lo = sb("m_lo", [P, KB * TOK], F32R)
        gains = sb("gains", [P, 4 * KB])
        b_f = sb("b_f", [HEADS, 1])
        ident = sb("ident", [P, P])
        ones = sb("ones", [P, P])
        rstd = sb("rstd", [P, TOK])
        mean = sb("mean", [P, TOK])
        ssq = sb("ssq", [P, TOK])
        sq = sb("sq", [P, TOK])
        neg_max = sb("neg_max", [P, 3])
        unused = sb("unused", [P, 1])
        exp_sum = sb("exp_sum", [P, 3])
        inv_sum = sb("inv_sum", [P, 3])
        f_query = sb("f_query", [P, 3])
        tmp = sb("tmp", [P, 6 * TOK])
        h = under("h", [P, KB * TOK])
        q_t = [sb(f"q_t{m}", [P, TOK]) for m in range(2)]
        k_t = [sb(f"k_t{m}", [P, KEYS]) for m in range(2)]
        v_t = [sb(f"v_t{m}", [P, NEW + TOK]) for m in range(2)]
        v_cache = [sb(f"v_cache{m}", [P, HD]) for m in range(2)]
        v_rows = sb("v_rows", [P, 3 * HD])
        bias = [sb(f"bias{m}", [P, P2]) for m in range(2)]
        f_keys = sb("f_keys", [P, KEYS])
        probs = sb("probs", [P, P2])
        probs_t = sb("probs_t", [P, 512])
        logf = sb("logf", [HEADS, KEYS])
        f_sum = f_keys

        banks = ctx.enter_context(nc.psum_tensor("banks", [P, 8, 512], F32))
        SCORES, SAMPLE, VALUES, TURNED = 4, 5, 6, 7
        o_acc = banks[:, SAMPLE, S1:S1 + TOK]

        bias_rows = nc.dram_tensor("bias_rows", [HEADS, P, 2 * P], F32).ap()
        f_rows = nc.dram_tensor("f_rows", [HEADS, KEYS], F32).ap()

        def blk(t, n, count=1):
            return t[:, bass.ds(n * TOK, count * TOK)]

        def tm(n, count=1):
            return tmp[:, n * TOK:(n + count) * TOK]

        def squares(c):
            return ple_part[:, c * 4 * TOK:(c + 1) * 4 * TOK]

        def gain(which, n):
            return gains[:, bass.ds(n + which * KB, 1)]

        def f32(ap):
            return ap.bitcast(F32)

        s_slab = [sem(f"slab_loaded{i}") for i in range(SLOTS)]
        s_whi = sem("slab_hi_ready")
        s_wlo = sem("slab_lo_ready")
        s_mul = sem("slab_multiplied")
        s_acc = sem("acc_read")
        s_x = [sem(f"x_chunk_loaded{i}") for i in range(4)]
        s_small = sem("gains_loaded")
        s_forget = sem("forget_inputs_loaded")
        s_h = sem("h_loaded")
        s_const = sem("constants_ready")
        s_zero = sem("pads_zeroed")
        s_xhi = sem("x_hi_ready")
        s_xlo = sem("x_split")
        s_ohi = sem("o_hi_ready")
        s_olo = sem("o_split")
        s_mhi = sem("m_hi_ready")
        s_mlo = sem("m_split")
        s_sq = sem("square_ready")
        s_ssq = sem("square_sum_ready")
        s_sqp = sem("x_squares_gpsimd")
        s_sqa = sem("x_squares_scalar")
        s_sqd = sem("x_squares_added")
        s_sum = sem("token_sum_ready")
        s_mean = sem("mean_ready")
        s_root = sem("root_ready")
        s_rstd = sem("rstd_ready")
        s_fdve = sem("forget_step_vector")
        s_fact = sem("forget_step_scalar")
        s_fst = sem("forget_sums_stored")
        s_brow = sem("bias_rows_stored")
        s_ld = [sem(f"unit_inputs_loaded{m}") for m in range(2)]
        s_kv = [sem(f"kv_stored{m}") for m in range(2)]
        s_decay = sem("decay_ready")
        s_bias = [sem(f"bias_ready{m}") for m in range(2)]
        s_score = sem("scores_ready")
        s_logit = sem("logits_ready")
        s_max = sem("max_ready")
        s_exp = sem("exp_ready")
        s_inv = sem("inverse_sum_ready")
        s_prob = sem("probs_ready")
        s_vcopy = sem("value_rows_ready")
        s_turn = sem("probs_turned")
        s_tcopy = sem("turned_probs_ready")
        s_pv = sem("attended")
        s_gate = sem("gate_ready")
        s_branch = sem("branch_a_gated")
        s_merged = sem("merged_ready")
        s_p = sem("p_loaded")
        s_sqr = sem("hidden_squared")
        s_pread = sem("ple_part_read")
        s_plep = sem("ple_gated")
        s_hfin = sem("h_final_ready")
        s_hg = sem("h_gained")
        s_y = [sem("y_ready_vector"), sem("y_ready_gpsimd")]
        s_out = sem("outputs_stored")
        s_pass = sem("wait_passed")

        def acc_count(t, add=1):
            return t.count(1, add - (2 if t.first >= T_GATE else 0))

        def scale_output(eng, first, blocks):
            out = h[:, first * TOK:(first + blocks) * TOK].rearrange("p (n t) -> p n t", n=blocks)
            return eng.tensor_tensor(out, out, rstd[:, :].unsqueeze(1).broadcast_to([P, blocks, TOK]), ALU.mult)

        def after(eng, s, value):
            if not isinstance(value, int) or value > 0:
                eng.wait_ge(s, value)

        def stand(eng, s, value):
            eng.wait_ge(s, value)
            eng.sem_inc(s_pass, 1)

        block = ctx.enter_context(nc.Block())

        @block.sync
        def _(sp):
            def load_x(c):
                sp.dma_start(h[:, c * 4 * TOK:(c + 1) * 4 * TOK], io["x_t"][:, c * 4 * TOK:(c + 1) * 4 * TOK]).then_inc(s_x[c], 16)

            def load_slab(s, slot):
                sp.dma_start(w_raw[:, slot, :], s).then_inc(s_slab[slot], 16)

            w = io["w_slabs"]
            sp.dma_start(gains[:, :], io["gains"]).then_inc(s_small, 16)
            load_slab(w[0], 0)
            load_x(0)
            load_x(1)
            load_slab(w[1], 1)
            load_x(2)
            load_x(3)
            load_slab(w[2], 2)
            load_slab(w[3], 3)
            slabs = 2 * T_END
            first = SLOTS + (slabs - SLOTS) % SLOTS
            for s in range(SLOTS, first):
                sp.wait_ge(s_wlo, s - SLOTS + 1)
                load_slab(w[s], s % SLOTS)
            with sp.Fori(0, (slabs - first) // SLOTS) as i:
                for j in range(SLOTS):
                    s = first + j
                    split = sp.snap(i * SLOTS + (s - SLOTS + 1))
                    sp.wait_ge(s_wlo, split)
                    load_slab(w[bass.ds(i * SLOTS + s, 1)].rearrange("a p n -> (a p) n"), s % SLOTS)

        @block.tensor
        def _(pe):
            def multiply(t, hi, lo, ready=None, value=None, bank_read=False, second=None, between=None):
                pe_bank = t.half
                if bank_read:
                    pe.wait_ge(s_acc, t.first - 1)
                for half in range(2):
                    if half and between:
                        between()
                    pe.wait_ge(s_wlo, t.count(2, half + 1))
                    slot = 2 * t.half + half
                    for kk in range(SLAB_KB):
                        k = half * SLAB_KB + kk
                        if k == KB - 1 and ready:
                            pe.wait_ge(ready, value)
                        bank = pe_bank if second is None or half == 0 else second
                        out = banks[:, bank, 0:TOK]
                        ws = slice(kk * P, (kk + 1) * P)
                        xs = slice(k * TOK, (k + 1) * TOK)
                        lo_k, hi_k = (0, KB - 1) if second is None else (half * SLAB_KB, half * SLAB_KB + SLAB_KB - 1)
                        nc.tensor.matmul(out, w_hi[:, slot, ws], hi[:, xs], start=k == lo_k, stop=False)
                        nc.tensor.matmul(out, w_hi[:, slot, ws], lo[:, xs], start=False, stop=False)
                        mm = nc.tensor.matmul(out, w_lo[:, slot, ws], hi[:, xs], start=False, stop=k == hi_k)
                    mm.then_inc(s_mul, 1)

            def token_sums(n, value):
                pe.wait_ge(s_ssq, value)
                nc.tensor.matmul(banks[:, SCORES, 0:TOK], ones[:, :], ssq[:, :], start=True, stop=True).then_inc(s_sum, 1)

            def scores(u):
                m = u.mixer
                q, k, v = q_t[m], k_t[m], v_t[m]
                pe.wait_ge(s_acc, u.count(3, T_UNIT + 3))
                pe.wait_ge(s_ld[m], u.head * 80 + 80)
                after(pe, s_logit, u.count(2))
                after(pe, s_olo, u.count())
                after(pe, s_vcopy, u.count())
                nc.tensor.matmul(banks[:, SCORES, 0:P], q[:, NEW:NEW + P], k[:, S1:S1 + P], start=True, stop=True)
                nc.tensor.matmul(banks[:, SCORES, P:P + SEQ], q[:, NEW + P:TOK], k[:, S1:KEYS], start=True, stop=True)
                nc.tensor.matmul(banks[0:NEW, SAMPLE, S0:S1], q[:, 0:NEW], k[:, 0:S1], start=True, stop=True)
                for j in range(3):
                    tr = nc.tensor.transpose(banks[:, VALUES, j * HD:(j + 1) * HD], v[:, j * P:(j + 1) * P], ident[:, :])
                tr.then_inc(s_score, 1)

            def turn(u):
                pe.wait_ge(s_prob, u.count(3, 3))
                after(pe, s_tcopy, u.count())
                b = banks[:, TURNED, :]
                nc.tensor.transpose(b[:, P:2 * P], probs[:, P0:P1], ident[:, :])
                nc.tensor.transpose(b[:, 2 * P:3 * P], probs[:, P1:P1 + P], ident[:, :])
                nc.tensor.transpose(b[:, 3 * P:4 * P], probs[:, P1 + P:P2], ident[:, :])
                nc.tensor.transpose(b[:, 0:NEW], probs[0:NEW, 0:P], ident[0:NEW, 0:NEW])
                nc.tensor.transpose(b[:, NEW:P], probs[0:NEW, NEW:NEW + P], ident[0:NEW, 0:NEW]).then_inc(s_turn, 1)

            def attend(u):
                pe.wait_ge(s_tcopy, u.count(1, 1))
                pe.wait_ge(s_vcopy, u.count(1, 1))
                pe.wait_ge(s_logit, u.count(2, 2))
                vc = v_cache[u.mixer]
                new, first, second = (v_rows[:, j * HD:(j + 1) * HD] for j in range(3))
                nc.tensor.matmul(o_acc[:, 0:NEW], vc[:, :], probs_t[:, 0:NEW], start=True, stop=False)
                nc.tensor.matmul(o_acc[:, 0:NEW], new, probs_t[:, NEW:P], start=False, stop=True)
                nc.tensor.matmul(o_acc[:, NEW:NEW + P], first, probs_t[:, P:2 * P], start=True, stop=True)
                nc.tensor.matmul(o_acc[:, NEW + P:TOK], first, probs_t[:, 2 * P:3 * P], start=True, stop=False)
                nc.tensor.matmul(o_acc[:, NEW + P:TOK], second, probs_t[:, 3 * P:4 * P], start=False, stop=True).then_inc(s_pv, 1)

            def mix_in(t, between=None, bank_read=False):
                multiply(t, x_hi, x_lo, between=between, bank_read=bank_read)

            def unit(t, before):
                mix_in(t)
                if before:
                    scores(before)
                mix_in(t.plus(1))
                mix_in(t.plus(2), between=(lambda: turn(before)) if before else None)
                if before:
                    attend(before)

            def merge(t, first=False):
                multiply(t, o_hi, o_lo, s_olo if first else None, UNITS, second=2 + t.half)

            pe.wait_ge(s_const, 3)
            for k in range(KB):
                pe.wait_ge(s_xlo, k + 1)
                if k % SLAB_KB == 0:
                    pe.wait_ge(s_wlo, k // SLAB_KB + 1)
                slot, kk = divmod(k, SLAB_KB)
                ws, xs = slice(kk * P, (kk + 1) * P), slice(k * TOK, (k + 1) * TOK)
                out = banks[:, 0, 0:TOK]
                nc.tensor.matmul(out, w_hi[:, slot, ws], x_hi[:, xs], start=k == 0, stop=False)
                nc.tensor.matmul(out, w_hi[:, slot, ws], x_lo[:, xs], start=False, stop=False)
                mm = nc.tensor.matmul(out, w_lo[:, slot, ws], x_hi[:, xs], start=False, stop=k == KB - 1)
                if kk == SLAB_KB - 1:
                    mm.then_inc(s_mul, 1)
            mix_in(Panel(T_UNIT), between=lambda: token_sums(0, 1))
            mix_in(Panel(T_UNIT + 1), bank_read=True)
            mix_in(Panel(T_UNIT + 2), bank_read=True)
            unit(Panel(T_UNIT + 3), Unit(0, 0))
            with pe.Fori(1, HEADS) as i:
                t = Panel(T_UNIT, 6, i)
                unit(t, Unit(i - 1, 1))
                unit(t.plus(3), Unit(i, 0))
            last = Unit(HEADS - 1, 1)
            mix_in(Panel(T_MERGE))
            scores(last)
            mix_in(Panel(T_MERGE + 1))
            turn(last)
            pe_t = Panel(T_MERGE + 2)
            attend(last)
            merge(pe_t, first=True)
            mix_in(Panel(T_MERGE + 3))
            mix_in(Panel(T_MERGE + 4))
            merge(Panel(T_MERGE + 5))
            with pe.Fori(1, KB // 2) as i:
                t = Panel(T_MERGE, 6, i)
                for j in (0, 3):
                    mix_in(t.plus(j))
                    mix_in(t.plus(j + 1))
                    merge(t.plus(j + 2))
            with pe.Fori(0, KB // 2) as i:
                for j in range(2):
                    multiply(Panel(T_OUT + j, 2, i), m_hi, m_lo, None if j else s_mlo, KB)

            def up(t, first=False):
                multiply(t, x_hi, x_lo, s_xlo if first else None, 2 * KB)

            def down(t, quarter):
                multiply(t, o_hi, o_lo, None if t.half == (T_FF + 1) % 2 else s_olo, quarter * KB + 2 * KB)

            up(Panel(T_FF), first=True)
            token_sums(1, 1 + KB)
            up(Panel(T_FF + 1))
            with pe.Fori(1, KB // 2) as i:
                for j in range(2):
                    up(Panel(T_FF + j, 2, i))
            with pe.Fori(0, KB // 2) as i:
                for j in range(2):
                    down(Panel(T_FF + KB + j, 2, i), 0)
            with pe.Fori(1, QUARTERS) as quarter:
                with pe.Fori(0, KB // 2) as i:
                    for j in range(2):
                        up(Panel(T_FF + j, 2, quarter * KB + i))
                with pe.Fori(0, KB // 2) as i:
                    for j in range(2):
                        down(Panel(T_FF + KB + j, 2, quarter * KB + i), quarter)

            pe.wait_ge(s_acc, T_PLE)
            pe.wait_ge(s_mlo, KB + 2)
            for s in range(4):
                pe.wait_ge(s_wlo, 2 * T_PLE + s + 1)
                after(pe, s_pread, s - 1)
                for n in range(4):
                    out = banks[:, 4 * (s % 2) + n, 0:TOK]
                    for k in range(2):
                        b = 2 * n + k
                        slot = (2 * T_PLE + s) % SLOTS
                        ws, xs = slice(b * P, (b + 1) * P), slice(k * TOK, (k + 1) * TOK)
                        nc.tensor.matmul(out, w_hi[:, slot, ws], m_hi[:, xs], start=k == 0, stop=False)
                        nc.tensor.matmul(out, w_hi[:, slot, ws], m_lo[:, xs], start=False, stop=False)
                        mm = nc.tensor.matmul(out, w_lo[:, slot, ws], m_hi[:, xs], start=False, stop=k == 1)
                mm.then_inc(s_mul, 1)

            def gate(t):
                multiply(t, x_hi, x_lo)

            pe.wait_ge(s_pread, 4)
            token_sums(2, 1 + 2 * KB)
            gate(Panel(T_GATE))
            gate(Panel(T_GATE + 1))
            with pe.Fori(1, KB // 2) as i:
                for j in range(2):
                    gate(Panel(T_GATE + j, 2, i))
            token_sums(3, 1 + 3 * KB)

        @block.scalar
        def _(act):
            def split_weights(t, halves=(0, 1)):
                for half in halves:
                    slot = 2 * t.half + half
                    act.wait_ge(s_slab[slot], t.loads())
                    after(act, s_mul, t.count(2, half - SLOTS + 1))
                    nc.scalar.activation(w_hi[:, slot, :], w_raw[:, slot, :], ACT.Copy).then_inc(s_whi, 1)

            def root(n):
                act.wait_ge(s_mean, n)
                nc.scalar.activation(mean[:, :], mean[:, :], ACT.Sqrt).then_inc(s_root, 1)

            def ready_root():
                nc.scalar.activation(unused[:, :], ones[:, 0:1], ACT.Sqrt)

            def load_unit(u):
                m, i = u.mixer, u.head
                after(act, s_score, u.count(1, -1))
                after(act, s_logit, u.count(2, -2))
                after(act, s_pv, u.count(1, -1))

                def head(t):
                    return t[bass.ds(i, 1)].rearrange("a p n -> (a p) n")

                if m == 0:
                    rows = head(bias_rows)
                    act.dma_start(bias[0][:, 0:S1], rows[:, 0:S1]).then_inc(s_ld[0], 16)
                    act.dma_start(bias[0][:, P0:P1], rows[:, P:2 * P]).then_inc(s_ld[0], 16)
                    act.dma_start(bias[0][:, P1:P2], rows[:, :]).then_inc(s_ld[0], 16)
                else:
                    after(act, s_bias[1], i * 3)
                    act.dma_start(f_keys[:, :], f_rows[bass.ds(i, 1), :].broadcast_to([P, KEYS])).then_inc(s_ld[1], 16)
                    act.dma_start(f_query[:, 1:3], bass.AP(tensor=f_rows.tensor, offset=i * KEYS + S1,
                                                           ap=[[1, P], [P, 2]]),
                                  allow_slow_non_contiguous=True).then_inc(s_ld[1], 16)
                    act.dma_start(f_query[0:NEW, 0:1], bass.AP(tensor=f_rows.tensor, offset=i * KEYS + PAST,
                                                               ap=[[1, NEW], [1, 1]]),
                                  allow_slow_non_contiguous=True).then_inc(s_ld[1], 16)
                act.dma_start(k_t[m][:, 0:PAST], head(io["k_cache_t"][m])).then_inc(s_ld[m], 16)
                act.dma_start(v_cache[m][:, :], head(io["v_cache"][m])).then_inc(s_ld[m], 16)

            def store_kv(u):
                m, i = u.mixer, u.head
                act.wait_ge(s_acc, u.count(3, T_UNIT + 3))
                for j, src in ((0, k_t[m][:, PAST:KEYS]), (1, v_t[m][:, NEW:NEW + TOK])):
                    out = io["kv_t"][2 * m + j][bass.ds(i, 1)].rearrange("a p n -> (a p) n")
                    act.dma_start(out, src).then_inc(s_kv[m], 16)

            def exps(u):
                act.wait_ge(s_score, u.count(1, 1))
                after(act, s_pv, u.count())
                nc.scalar.activation(v_rows[:, :], banks[:, VALUES, 0:3 * HD], ACT.Copy).then_inc(s_vcopy, 1)
                after(act, s_inv, u.count())
                for n, (rows, c, a, b) in enumerate(((P, 1, P0, P1), (P, 2, P1, P2), (NEW, 0, S0, S1))):
                    act.wait_ge(s_max, u.count(3, n + 1))
                    nc.scalar.activation(probs[0:rows, a:b], probs[0:rows, a:b], ACT.Exp, bias=neg_max[0:rows, c:c + 1],
                                         accum_out=exp_sum[0:rows, c:c + 1]).then_inc(s_exp, 1)

            def copy_turned(u):
                act.wait_ge(s_turn, u.count(1, 1))
                after(act, s_pv, u.count())
                nc.scalar.activation(probs_t[:, :], banks[:, TURNED, :], ACT.Copy).then_inc(s_tcopy, 1)

            def split_output(u):
                stand(act, s_pv, u.count(1, 1))
                nc.scalar.activation(blk(o_hi, u.head + HEADS * u.mixer), o_acc, ACT.Copy).then_inc(s_ohi, 1)

            act.dma_start(b_f[:, :], io["b_f"]).then_inc(s_forget, 16)
            act.dma_start(logf[:, 0:PAST], io["logf_cache_t"]).then_inc(s_forget, 16)
            act.wait_ge(s_small, 16)
            for n in range(KB):
                if n % 4 == 0:
                    act.wait_ge(s_x[n // 4], 16)
                if n in (0, 6):
                    split_weights(Panel(0), (n // 6,))
                nc.scalar.activation(blk(x_hi, n), blk(h, n), ACT.Copy, scale=gain(MIX, n)).then_inc(s_xhi, 1)
                if n in (11, 15):
                    nc.scalar.activation(squares(n // 4), blk(h, n - 3, 4), ACT.Square).then_inc(s_sqa, 1)
            rel = io["rel_rows"]
            act.dma_start(bias_rows, bass.AP(tensor=rel.tensor, offset=P - 1, ap=[[BIAS_ROW, HEADS], [-1, P], [1, 2 * P]])).then_inc(s_brow, 16)
            act.dma_start(io["rolled"][0], io["cache_a_k"][PAST - CHUNK:PAST, :]).then_inc(s_out, 16)
            act.dma_start(io["rolled"][1], io["cache_a_v"][PAST - CHUNK:PAST, :]).then_inc(s_out, 16)
            split_weights(Panel(1))

            act.wait_ge(s_const, 3)
            ready_root()
            split_weights(Panel(2))
            root(1)
            split_weights(Panel(3))
            act.wait_ge(s_xlo, KB)
            act.wait_ge(s_ssq, 1)
            act.wait_ge(s_brow, 16)
            load_unit(Unit(0, 0))
            act.wait_ge(s_fdve, 3)
            nc.scalar.activation(tm(3)[0:HEADS], tm(2)[0:HEADS], ACT.Exp, scale=-1.0).then_inc(s_fact, 1)
            act.wait_ge(s_fdve, 4)
            nc.scalar.activation(tm(5)[0:HEADS], tm(4)[0:HEADS], ACT.Ln).then_inc(s_fact, 1)
            split_weights(Panel(4))
            act.wait_ge(s_fdve, 14)
            act.dma_start(io["logf_t"], logf[:, PAST:KEYS]).then_inc(s_out, 16)
            act.dma_start(f_rows, f_sum[0:HEADS, :]).then_inc(s_fst, 16)
            split_weights(Panel(5))

            def unit(t, before, this):
                split_weights(t.plus(2))
                load_unit(this)
                store_kv(before)
                exps(before)
                split_weights(t.plus(3))
                split_weights(t.plus(4), (0,))
                copy_turned(before)
                split_weights(t.plus(4), (1,))
                split_output(before)

            act.wait_ge(s_fst, 16)
            unit(Panel(T_UNIT + 3), Unit(0, 0), Unit(0, 1))
            with act.Fori(1, HEADS) as i:
                t = Panel(T_UNIT, 6, i)
                unit(t, Unit(i - 1, 1), Unit(i, 0))
                unit(t.plus(3), Unit(i, 0), Unit(i, 1))

            def sigmoid(t, src, dst):
                act.wait_ge(s_acc, acc_count(t))
                nc.scalar.activation(tm(dst), tm(src), ACT.Sigmoid).then_inc(s_gate, 1)

            def merged(n):
                stand(act, s_merged, n + 1)
                nc.scalar.activation(blk(m_hi, n), tm(4), ACT.Copy).then_inc(s_mhi, 1)

            def merge(t, n):
                split_weights(t.plus(2))
                sigmoid(t, 0, 1)
                split_weights(t.plus(3))
                sigmoid(t.plus(1), 2, 3)
                split_weights(t.plus(4))
                merged(n)

            last = Unit(HEADS - 1, 1)
            t = Panel(T_MERGE)
            split_weights(t.plus(2))
            store_kv(last)
            exps(last)
            sigmoid(t, 0, 1)
            split_weights(t.plus(3))
            copy_turned(last)
            sigmoid(t.plus(1), 2, 3)
            split_output(last)
            split_weights(t.plus(4))
            merged(0)
            merge(Panel(T_MERGE + 3), 1)
            act.wait_ge(s_olo, UNITS)
            act.wait_ge(s_kv[0], 32 * HEADS)
            act.wait_ge(s_kv[1], 32 * HEADS)
            act.dma_start(h[:, :], io["x_t"]).then_inc(s_h, 16)
            with act.Fori(1, KB // 2) as i:
                t = Panel(T_MERGE, 6, i)
                merge(t, i * 2)
                merge(t.plus(3), i * 2 + 1)

            def residual(t, n, which):
                stand(act, s_acc, acc_count(t))
                nc.scalar.activation(blk(x_hi, n), blk(h, n), ACT.Copy, scale=gain(which, n)).then_inc(s_xhi, 1)

            with act.Fori(0, KB // 2) as i:
                for j in range(2):
                    t = Panel(T_OUT + j, 2, i)
                    split_weights(t.plus(2))
                    residual(t, i * 2 + j, MLP)

            def hidden(t, number, n):
                split_weights(t.plus(2))
                stand(act, s_sqr, number + 1)
                nc.scalar.activation(blk(o_hi, n), tm(1), ACT.Copy).then_inc(s_ohi, 1)

            act.wait_ge(s_mul, 2 * T_FF)
            act.wait_ge(s_xlo, 2 * KB)
            act.dma_start(tm(4, 2), io["p_t"]).then_inc(s_p, 16)
            split_weights(Panel(T_FF + 2))
            root(2)
            act.wait_ge(s_sqr, 1)
            nc.scalar.activation(blk(o_hi, 0), tm(1), ACT.Copy).then_inc(s_ohi, 1)
            act.wait_ge(s_p, 16)
            nc.scalar.activation(m_hi[:, 0:2 * TOK], tm(4, 2), ACT.Copy).then_inc(s_mhi, 1)
            hidden(Panel(T_FF + 1), 1, 1)
            with act.Fori(1, KB // 2) as i:
                for j in range(2):
                    hidden(Panel(T_FF + j, 2, i), i * 2 + j, i * 2 + j)
            with act.Fori(0, KB // 2) as i:
                for j in range(2):
                    split_weights(Panel(T_FF + KB + j + 2, 2, i))
            with act.Fori(1, QUARTERS - 1) as quarter:
                with act.Fori(0, KB // 2) as i:
                    for j in range(2):
                        hidden(Panel(T_FF + j, 2, quarter * KB + i), quarter * KB + i * 2 + j, i * 2 + j)
                with act.Fori(0, KB // 2) as i:
                    for j in range(2):
                        split_weights(Panel(T_FF + KB + j + 2, 2, quarter * KB + i))
            tq = T_FF + (QUARTERS - 1) * 2 * KB
            with act.Fori(0, KB // 2) as i:
                for j in range(2):
                    hidden(Panel(tq + j, 2, i), i * 2 + (QUARTERS - 1) * KB + j, i * 2 + j)
            with act.Fori(0, KB // 2) as i:
                for j in range(2):
                    t = Panel(tq + KB + j, 2, i)
                    split_weights(t.plus(2))
                    residual(t, i * 2 + j, PLE)

            for s in range(4):
                act.wait_ge(s_mul, 2 * T_PLE + s + 1)
                g = 4 * (s % 2)
                nc.scalar.activation(ple_part[:, s * 4 * TOK:(s + 1) * 4 * TOK].rearrange("p (n t) -> p n t", n=4),
                                     banks[:, g:g + 4, 0:TOK], ACT.Copy).then_inc(s_pread, 1)
                split_weights(Panel(T_PLE + 2 + s // 2), (s % 2,))
            root(3)

            def gate(t, n, ahead):
                if ahead:
                    split_weights(t.plus(2))
                sigmoid(t, 0, 1)
                stand(act, s_sq, n + (2 * KB + 1))
                nc.scalar.activation(blk(h, n), blk(h, n), ACT.Copy, scale=gain(FINAL, n)).then_inc(s_hg, 1)

            with act.Fori(0, KB // 2 - 1) as i:
                for j in range(2):
                    gate(Panel(T_GATE + j, 2, i), i * 2 + j, True)
            for n in (KB - 2, KB - 1):
                gate(Panel(T_GATE + n), n, False)
            ready_root()
            root(4)
            for n, (first, blocks, ready) in enumerate(Y_CHUNKS):
                act.wait_ge(s_y[ready], sum(c[2] == ready for c in Y_CHUNKS[:n + 1]))
                cols = slice(first * TOK, (first + blocks) * TOK)
                act.dma_start(io["y_t"][:, cols], h[:, cols]).then_inc(s_out, 16)
            act.wait_ge(s_out, 16 * (3 + len(Y_CHUNKS)))

        @block.vector
        def _(dve):
            def split_weights(t, halves=(0, 1)):
                for half in halves:
                    slot = 2 * t.half + half
                    dve.wait_ge(s_whi, t.count(2, half + 1))
                    nc.vector.tensor_tensor(w_lo[:, slot, :], w_raw[:, slot, :], f32(w_hi[:, slot, :]), ALU.subtract).then_inc(s_wlo, 1)

            def summed(t):
                dve.wait_ge(s_mul, t.count(2, 2))
                return banks[:, t.half, 0:TOK]

            def inverse_rms(n):
                dve.wait_ge(s_sum, n)
                nc.vector.tensor_scalar(mean[:, :], banks[:, SCORES, 0:TOK], 1.0 / D_MODEL, EPS, ALU.mult, ALU.add).then_inc(s_mean, 1)
                dve.wait_ge(s_root, n)
                nc.vector.reciprocal(rstd[:, :], mean[:, :]).then_inc(s_rstd, 1)
                dve.wait_ge(s_rstd, n)

            def split_input(n, which, number):
                dve.wait_ge(s_xhi, number + 1)
                nc.vector.scalar_tensor_tensor(out=blk(x_lo, n), in0=blk(h, n), scalar=gain(which, n), in1=f32(blk(x_hi, n)),
                                               op0=ALU.mult, op1=ALU.subtract).then_inc(s_xlo, 1)

            def evacuate(t, u, what):
                acc = summed(t)
                m = u.mixer
                after(dve, s_score, u.count(1, -1))
                if what == 0:
                    nc.vector.scalar_tensor_tensor(out=q_t[m][:, :], in0=acc, scalar=SCALE, in1=rstd[:, :],
                                                   op0=ALU.mult, op1=ALU.mult).then_inc(s_acc, 1)
                    return
                after(dve, s_kv[m], u.head * 32)
                out = k_t[m][:, PAST:KEYS] if what == 1 else v_t[m][:, NEW:NEW + TOK]
                nc.vector.tensor_tensor(out, acc, rstd[:, :], ALU.mult).then_inc(s_acc, 1)

            def logits(u):
                m = u.mixer
                dve.wait_ge(s_score, u.count(1, 1))
                dve.wait_ge(s_bias[m], u.head * (2 + m) + (2 + m))
                after(dve, s_turn, u.count())
                nc.vector.tensor_tensor(probs[:, P0:P2], banks[:, SCORES, 0:P2 - P0], bias[m][:, P0:P2], ALU.add).then_inc(s_logit, 1)
                nc.vector.tensor_tensor(probs[0:NEW, S0:S1], banks[0:NEW, SAMPLE, S0:S1], bias[m][0:NEW, S0:S1], ALU.add).then_inc(s_logit, 1)
                for n, (rows, c, a, b) in enumerate(((P, 1, P0, P1), (P, 2, P1, P2), (NEW, 0, S0, S1))):
                    if n != 1:
                        dve.wait_ge(s_logit, u.count(2, 1 + (n == 2)))
                    nc.vector.tensor_reduce(neg_max[0:rows, c:c + 1], probs[0:rows, a:b], AX_X, ALU.max, negate=True).then_inc(s_max, 1)

            def invert(u):
                dve.wait_ge(s_exp, u.count(3, 3))
                after(dve, s_prob, u.count(3))
                nc.vector.reciprocal(inv_sum[:, :], exp_sum[:, :]).then_inc(s_inv, 1)

            def split_output(u):
                dve.wait_ge(s_ohi, u.count(1, 1))
                n = u.head + HEADS * u.mixer
                nc.vector.tensor_tensor(blk(o_lo, n), o_acc, f32(blk(o_hi, n)), ALU.subtract).then_inc(s_olo, 1)

            nc.vector.memset(exp_sum[:, :], 1.0).then_inc(s_zero, 1)
            dve.wait_ge(s_small, 16)
            for n in range(KB):
                if n in (0, 6):
                    split_weights(Panel(0), (n // 6,))
                split_input(n, MIX, n)
            split_weights(Panel(1))
            dve.wait_ge(s_sqa, 2)
            nc.vector.tensor_tensor(squares(2), squares(2), squares(3), ALU.add).then_inc(s_sqd, 1)
            dve.wait_ge(s_sqd, 1)
            dve.wait_ge(s_sqp, 3)
            nc.vector.tensor_tensor(squares(0), squares(0), squares(2), ALU.add).then_inc(s_sqd, 1)
            dve.wait_ge(s_sqd, 2)
            nc.vector.tensor_tensor(blk(ple_part, 0, 2), blk(ple_part, 0, 2), blk(ple_part, 2, 2), ALU.add).then_inc(s_sqd, 1)
            dve.wait_ge(s_sqd, 3)
            nc.vector.tensor_tensor(ssq[:, :], blk(ple_part, 0), blk(ple_part, 1), ALU.add).then_inc(s_ssq, 1)

            split_weights(Panel(2))
            inverse_rms(1)
            lf = [tm(n)[0:HEADS] for n in range(6)]
            nc.vector.tensor_tensor(lf[0], summed(Panel(0))[0:HEADS], rstd[0:HEADS, :], ALU.mult).then_inc(s_acc, 1)
            split_weights(Panel(3))
            dve.wait_ge(s_xlo, KB)
            dve.wait_ge(s_ssq, 1)
            for m in range(2):
                nc.vector.memset(v_t[m][:, 0:NEW], 0.0).then_inc(s_zero, 1)
            evacuate(Panel(T_UNIT), Unit(0, 0), 0)
            def step(ins, n):
                ins.then_inc(s_fdve, 1)
                dve.wait_ge(s_fdve, n)

            dve.wait_ge(s_acc, 1)
            dve.wait_ge(s_forget, 32)
            step(nc.vector.tensor_scalar(lf[1], lf[0], b_f[:, 0:1], None, ALU.add), 1)
            step(nc.vector.scalar_tensor_tensor(out=lf[2], in0=lf[1], scalar=-1.0, in1=lf[1], op0=ALU.mult, op1=ALU.max), 2)
            step(nc.vector.memset(probs[0:HEADS, 0:SEQ], 1.0), 3)
            dve.wait_ge(s_fact, 1)
            step(nc.vector.tensor_scalar(lf[4], lf[3], 1.0, None, ALU.add), 4)
            step(nc.vector.tensor_scalar(lf[0], lf[4], -1.0, None, ALU.add), 5)
            step(nc.vector.tensor_scalar(lf[2], lf[0], 1e-30, None, ALU.max), 6)
            step(nc.vector.reciprocal(lf[2], lf[2]), 7)
            dve.wait_ge(s_fact, 2)
            step(nc.vector.tensor_tensor(lf[5], lf[5], lf[2], ALU.mult), 8)
            step(nc.vector.tensor_tensor(lf[5], lf[5], lf[3], ALU.mult), 9)
            step(nc.vector.scalar_tensor_tensor(out=lf[0], in0=lf[0], scalar=0.0, in1=lf[3], op0=ALU.is_equal, op1=ALU.mult), 10)
            step(nc.vector.tensor_tensor(lf[5], lf[5], lf[0], ALU.add), 11)
            step(nc.vector.scalar_tensor_tensor(out=logf[:, PAST:KEYS], in0=lf[1], scalar=0.0, in1=lf[5], op0=ALU.min, op1=ALU.subtract), 12)
            one = probs[0:HEADS, 0:SEQ]
            step(nc.vector.tensor_tensor_scan(f_sum[0:HEADS, 0:S1], one[:, 0:S1], logf[:, 0:S1], 0.0, ALU.mult, ALU.add), 13)
            step(nc.vector.tensor_tensor_scan(f_sum[0:HEADS, S1:KEYS], one, logf[:, S1:KEYS], 0.0, ALU.mult, ALU.add), 14)
            evacuate(Panel(T_UNIT + 1), Unit(0, 0), 1)
            split_weights(Panel(4))
            evacuate(Panel(T_UNIT + 2), Unit(0, 0), 2)
            split_weights(Panel(5))

            def unit(t, before, this):
                evacuate(t, this, 0)
                split_weights(t.plus(2), (0,))
                logits(before)
                split_weights(t.plus(2), (1,))
                invert(before)
                evacuate(t.plus(1), this, 1)
                split_weights(t.plus(3))
                evacuate(t.plus(2), this, 2)
                split_weights(t.plus(4), (0,))
                split_output(before)
                split_weights(t.plus(4), (1,))

            unit(Panel(T_UNIT + 3), Unit(0, 0), Unit(0, 1))
            with dve.Fori(1, HEADS) as i:
                t = Panel(T_UNIT, 6, i)
                unit(t, Unit(i - 1, 1), Unit(i, 0))
                unit(t.plus(3), Unit(i, 0), Unit(i, 1))

            def gate_logits(t, dst):
                nc.vector.tensor_tensor(tm(dst), summed(t), rstd[:, :], ALU.mult).then_inc(s_acc, 1)

            def merge(t, n):
                acc = summed(t)
                dve.wait_ge(s_gate, n * 2 + 2)
                nc.vector.tensor_tensor(tm(4), acc, tm(1), ALU.mult).then_inc(s_branch, 1)
                nc.vector.tensor_tensor(tm(5), banks[:, 2 + t.half, 0:TOK], tm(3), ALU.mult).then_inc(s_acc, 1)
                dve.wait_ge(s_branch, n + 1)
                dve.wait_ge(s_acc, acc_count(t))
                nc.vector.tensor_tensor(tm(4), tm(4), tm(5), ALU.add).then_inc(s_merged, 1)
                dve.wait_ge(s_mhi, n + 1)
                nc.vector.tensor_tensor(blk(m_lo, n), tm(4), f32(blk(m_hi, n)), ALU.subtract).then_inc(s_mlo, 1)

            def merge_all(t, n):
                gate_logits(t, 0)
                split_weights(t.plus(2))
                gate_logits(t.plus(1), 2)
                split_weights(t.plus(3))
                merge(t.plus(2), n)
                split_weights(t.plus(4))

            last = Unit(HEADS - 1, 1)
            t = Panel(T_MERGE)
            gate_logits(t, 0)
            split_weights(t.plus(2), (0,))
            logits(last)
            split_weights(t.plus(2), (1,))
            invert(last)
            gate_logits(t.plus(1), 2)
            split_weights(t.plus(3))
            split_output(last)
            merge(t.plus(2), 0)
            split_weights(t.plus(4))
            merge_all(Panel(T_MERGE + 3), 1)
            with dve.Fori(1, KB // 2) as i:
                t = Panel(T_MERGE, 6, i)
                merge_all(t, i * 2)
                merge_all(t.plus(3), i * 2 + 1)

            def add_to_h(t, n):
                nc.vector.tensor_tensor(blk(h, n), summed(t), blk(h, n), ALU.add).then_inc(s_acc, 1)

            dve.wait_ge(s_h, 16)
            with dve.Fori(0, KB // 2) as i:
                for j in range(2):
                    t = Panel(T_OUT + j, 2, i)
                    add_to_h(t, i * 2 + j)
                    split_input(i * 2 + j, MLP, i * 2 + (KB + j))
                    split_weights(t.plus(2))

            def hidden(t, number, n):
                acc = summed(t)
                nc.vector.scalar_tensor_tensor(out=tm(0), in0=acc, scalar=0.0, in1=rstd[:, :],
                                               op0=ALU.max, op1=ALU.mult).then_inc(s_acc, 1)
                dve.wait_ge(s_ohi, number + (UNITS + 1))
                nc.vector.tensor_tensor(blk(o_lo, n), tm(1), f32(blk(o_hi, n)), ALU.subtract).then_inc(s_olo, 1)

            inverse_rms(2)
            hidden(Panel(T_FF), 0, 0)
            split_weights(Panel(T_FF + 2))
            dve.wait_ge(s_mhi, KB + 1)
            nc.vector.tensor_tensor(m_lo[:, 0:2 * TOK], tm(4, 2), f32(m_hi[:, 0:2 * TOK]), ALU.subtract).then_inc(s_mlo, 2)
            hidden(Panel(T_FF + 1), 1, 1)
            split_weights(Panel(T_FF + 3))
            with dve.Fori(1, KB // 2) as i:
                for j in range(2):
                    t = Panel(T_FF + j, 2, i)
                    hidden(t, i * 2 + j, i * 2 + j)
                    split_weights(t.plus(2))
            with dve.Fori(0, KB // 2) as i:
                for j in range(2):
                    t = Panel(T_FF + KB + j, 2, i)
                    add_to_h(t, i * 2 + j)
                    split_weights(t.plus(2))
            with dve.Fori(1, QUARTERS - 1) as quarter:
                with dve.Fori(0, KB // 2) as i:
                    for j in range(2):
                        t = Panel(T_FF + j, 2, quarter * KB + i)
                        hidden(t, quarter * KB + i * 2 + j, i * 2 + j)
                        split_weights(t.plus(2))
                with dve.Fori(0, KB // 2) as i:
                    for j in range(2):
                        t = Panel(T_FF + KB + j, 2, quarter * KB + i)
                        add_to_h(t, i * 2 + j)
                        split_weights(t.plus(2))
            tq = T_FF + (QUARTERS - 1) * 2 * KB
            with dve.Fori(0, KB // 2) as i:
                for j in range(2):
                    t = Panel(tq + j, 2, i)
                    hidden(t, i * 2 + (QUARTERS - 1) * KB + j, i * 2 + j)
                    split_weights(t.plus(2))
            with dve.Fori(0, KB // 2) as i:
                for j in range(2):
                    t = Panel(tq + KB + j, 2, i)
                    add_to_h(t, i * 2 + j)
                    split_input(i * 2 + j, PLE, i * 2 + (2 * KB + j))
                    split_weights(t.plus(2))
            split_weights(Panel(T_PLE + 2))
            split_weights(Panel(T_PLE + 3))
            inverse_rms(3)

            def gate(t, n, ahead):
                gate_logits(t, 0)
                if ahead:
                    split_weights(t.plus(2))
                dve.wait_ge(s_gate, n + (2 * KB + 1))
                nc.vector.tensor_tensor(tm(2), tm(1), blk(ple_part, n), ALU.mult).then_inc(s_plep, 1)
                dve.wait_ge(s_plep, n + 1)
                nc.vector.tensor_tensor(blk(h, n), blk(h, n), tm(2), ALU.add).then_inc(s_hfin, 1)

            dve.wait_ge(s_pread, 4)
            with dve.Fori(0, KB // 2 - 1) as i:
                for j in range(2):
                    gate(Panel(T_GATE + j, 2, i), i * 2 + j, True)
            for n in (KB - 2, KB - 1):
                gate(Panel(T_GATE + n), n, False)
            inverse_rms(4)
            dve.wait_ge(s_hg, KB)
            for first, blocks, by in Y_CHUNKS:
                if by == 0:
                    scale_output(nc.vector, first, blocks).then_inc(s_y[0], 1)

        @block.gpsimd
        def _(pool):
            nc.gpsimd.memset(ident[:, :], 0.0).then_inc(s_const, 1)
            nc.gpsimd.memset(ones[:, :], 1.0).then_inc(s_const, 1)
            pool.wait_ge(s_const, 1)
            nc.gpsimd.affine_select(out=ident[:, :], in_=ident[:, :], compare_op=ALU.not_equal, fill=1.0, base=0,
                                    pattern=[[-1, P]], channel_multiplier=1).then_inc(s_const, 1)
            for c in range(2):
                pool.wait_ge(s_x[c], 16)
                nc.gpsimd.tensor_tensor(squares(c), blk(h, 4 * c, 4), blk(h, 4 * c, 4), ALU.mult).then_inc(s_sqp, 1)
            pool.wait_ge(s_sqp, 2)
            nc.gpsimd.tensor_tensor(squares(0), squares(0), squares(1), ALU.add).then_inc(s_sqp, 1)

            def make_bias(u):
                m, i = u.mixer, u.head
                b = bias[m]
                stand(pool, s_ld[m], i * 80 + 80)
                if m == 0:
                    nc.gpsimd.memset(b[0:CHUNK, P1 - CHUNK:P1], NEG).then_inc(s_bias[0], 1)
                    nc.gpsimd.memset(b[0:CHUNK, P2 - CHUNK:P2], NEG).then_inc(s_bias[0], 1)
                    return
                parts = ((NEW, 0, S0, S1, 0, PAST), (P, 1, P0, P1, S1, 0), (P, 2, P1, P2, S1, P))
                for rows, c, a, e, key, base in parts:
                    nc.gpsimd.tensor_scalar(b[0:rows, a:e], f_keys[0:rows, key:key + e - a], -1.0, f_query[0:rows, c:c + 1],
                                            ALU.mult, ALU.add).then_inc(s_decay, 1)
                stand(pool, s_decay, i * 3 + 3)
                for rows, c, a, e, key, base in parts:
                    nc.gpsimd.affine_select(out=b[0:rows, a:e], in_=b[0:rows, a:e], compare_op=ALU.is_ge, fill=NEG, base=base,
                                            pattern=[[-1, e - a]], channel_multiplier=1).then_inc(s_bias[1], 1)

            def normalise(u):
                stand(pool, s_inv, u.count(1, 1))
                for rows, c, a, e in ((P, 1, P0, P1), (P, 2, P1, P2), (NEW, 0, S0, S1)):
                    nc.gpsimd.tensor_scalar(probs[0:rows, a:e], probs[0:rows, a:e], inv_sum[0:rows, c:c + 1], None, ALU.mult).then_inc(s_prob, 1)

            make_bias(Unit(0, 0))
            with pool.Fori(0, HEADS - 1) as i:
                normalise(Unit(i, 0))
                make_bias(Unit(i, 1))
                normalise(Unit(i, 1))
                make_bias(Unit(i + 1, 0))
            normalise(Unit(HEADS - 1, 0))
            make_bias(Unit(HEADS - 1, 1))
            normalise(Unit(HEADS - 1, 1))

            def add_squares(done, ready, value):
                pool.wait_ge(s_sum, done + 1)
                nc.gpsimd.memset(ssq[:, :], 0.0).then_inc(s_sqp, 1)
                pool.wait_ge(s_sqp, cleared[done])
                with pool.Fori(0, KB) as n:
                    stand(pool, s_ssq, n + (done * KB + 1))
                    stand(pool, ready, n + value)
                    nc.gpsimd.tensor_tensor(sq[:, :], blk(h, n), blk(h, n), ALU.mult).then_inc(s_sq, 1)
                    pool.wait_ge(s_sq, n + (done * KB + 1))
                    nc.gpsimd.tensor_tensor(ssq[:, :], ssq[:, :], sq[:, :], ALU.add).then_inc(s_ssq, 1)

            cleared = {done: 4 + done for done in range(3)}
            add_squares(0, s_acc, T_OUT + 1)
            with pool.Fori(0, QUARTERS) as quarter:
                with pool.Fori(0, KB) as n:
                    pool.wait_ge(s_acc, quarter * (2 * KB) + n + (T_FF + 1))
                    nc.gpsimd.tensor_tensor(tm(1), tm(0), tm(0), ALU.mult).then_inc(s_sqr, 1)
            add_squares(1, s_acc, T_PLE - KB + 1)
            add_squares(2, s_hfin, 1)
            pool.wait_ge(s_rstd, 4)
            pool.wait_ge(s_hg, KB)
            for first, blocks, by in Y_CHUNKS:
                if by == 1:
                    scale_output(nc.gpsimd, first, blocks).then_inc(s_y[1], 1)


def slabs_of(w):
    rows, cols = w.shape
    s = w.reshape(rows // SLAB, SLAB_KB, P, cols // P, P).transpose(3, 0, 2, 1, 4)
    return s.reshape(cols // P, rows // SLAB, P, SLAB)


def kernel(**inputs):
    import concourse.bacc as bacc
    from concourse.bass_utils import run_bass_kernel_spmd

    a = {k: np.asarray(v) for k, v in inputs.items()}
    f = np.float32
    w_in = a["w_in"][0]
    wa = HEADS * HD
    slabs = np.empty((2 * T_END, P, SLAB), f)

    def put(first, panels):
        slabs[2 * first:2 * first + 2 * len(panels)] = panels.reshape(-1, P, SLAB)

    logits = np.zeros((D_MODEL, P), f)
    logits[:, 0:HEADS] = w_in[:, 6 * wa:6 * wa + HEADS]
    put(T_FORGET, slabs_of(logits))
    qkv = slabs_of(w_in[:, 0:6 * wa]).reshape(2, 3, HEADS, 2, P, SLAB)
    put(T_UNIT, qkv.transpose(2, 0, 1, 3, 4, 5).reshape(-1, 2, P, SLAB))
    gates = slabs_of(w_in[:, 6 * wa + HEADS:]).reshape(2, KB, 2, P, SLAB)
    merge = np.stack([slabs_of(a["w_a_proj"][0])[:, 0], slabs_of(a["w_b_proj"][0])[:, 0]], 1)
    put(T_MERGE, np.stack([gates[0], gates[1], merge], 1).reshape(-1, 2, P, SLAB))
    put(T_OUT, slabs_of(a["w_o"][0]))
    up, down = a["w_up"][0], a["w_down"][0]
    for q in range(QUARTERS):
        part = slice(q * D_MODEL, (q + 1) * D_MODEL)
        put(T_FF + 2 * KB * q, slabs_of(up[:, part]))
        put(T_FF + 2 * KB * q + KB, slabs_of(down[part]))
    proj = a["w_ple_proj"][0].reshape(2, P, 4, 4, P).transpose(2, 1, 3, 0, 4).reshape(4, P, SLAB)
    put(T_PLE, proj.reshape(2, 2, P, SLAB))
    put(T_GATE, slabs_of(a["w_ple_gate"][0]))

    def by_block(sample, prompt):
        t = np.concatenate([sample.reshape(NEW, -1), prompt.reshape(SEQ, -1)], 0)
        return np.ascontiguousarray(t.T.reshape(-1, P, TOK).transpose(1, 0, 2).reshape(P, -1))

    gains = np.stack([a["g_mix"][0], a["g_mlp"][0], a["g_ple"][0], a["g_final"]], 0)
    table = a["rel_bias"][0][:, ::-1]
    rel = np.concatenate([np.repeat(table[:, 0:1], REL_CLIP - 1, 1), table], 1)[:, 0:BIAS_ROW]
    arrays = {
        "w_slabs": slabs,
        "x_t": by_block(a["x_sample"], a["x_prompt"]),
        "p_t": by_block(a["p_sample"], a["p_prompt"]),
        "gains": np.ascontiguousarray(gains.reshape(4, KB, P).transpose(2, 0, 1).reshape(P, 4 * KB)),
        "b_f": np.ascontiguousarray(a["b_f"].reshape(HEADS, 1)),
        "rel_rows": np.ascontiguousarray(rel),
        "logf_cache_t": np.ascontiguousarray(a["cache_b_logf"][0, 0].T),
        "k_cache_t": np.ascontiguousarray(np.stack([a["cache_a_k"][0, 0], a["cache_b_k"][0, 0]]).transpose(0, 2, 3, 1)),
        "v_cache": np.ascontiguousarray(np.stack([a["cache_a_v"][0, 0], a["cache_b_v"][0, 0]]).transpose(0, 2, 1, 3)),
        "cache_a_k": np.ascontiguousarray(a["cache_a_k"].reshape(PAST, wa)),
        "cache_a_v": np.ascontiguousarray(a["cache_a_v"].reshape(PAST, wa)),
    }
    outputs = {
        "y_t": (P, KB * TOK),
        "kv_t": (4, HEADS, P, TOK),
        "logf_t": (HEADS, TOK),
        "rolled": (2, NEW, wa),
    }
    nc = bacc.Bacc("TRN2", target_bir_lowering=False, num_devices=1)
    io = {n: nc.dram_tensor("in_" + n, v.shape, F32, kind="ExternalInput").ap() for n, v in arrays.items()}
    io |= {n: nc.dram_tensor("out_" + n, s, F32, kind="ExternalOutput").ap() for n, s in outputs.items()}
    hybrid_layer(nc, io)
    r = run_bass_kernel_spmd(nc, [{"in_" + n: v for n, v in arrays.items()}], core_ids=[0]).results[0]
    r = {n: r["out_" + n] for n in outputs}

    y = r["y_t"].reshape(P, KB, TOK).transpose(2, 1, 0).reshape(TOK, D_MODEL)
    kv = r["kv_t"].transpose(0, 3, 1, 2)
    lf = r["logf_t"].T
    rolled = r["rolled"].reshape(2, NEW, HEADS, HD)

    def prompt(t):
        return np.ascontiguousarray(t[NEW:])[None, None]

    def sample(t):
        return np.ascontiguousarray(t[0:NEW])[None, None]

    def band(j):
        return np.concatenate([rolled[j], kv[j][0:NEW]], 0)[None, None]

    return (np.ascontiguousarray(y[NEW:])[None], np.ascontiguousarray(y[0:NEW])[None],
            prompt(kv[0]), prompt(kv[1]), prompt(kv[2]), prompt(kv[3]), prompt(lf),
            band(0), band(1), sample(kv[2]), sample(kv[3]), sample(lf))
```
